# Optimizing a Trainium2 kernel written in Bass

```python
import math
import jax, jax.numpy as jnp
from jax import lax
import numpy as np

D_MODEL = 2048
BATCH = 1
SEQ = 256
DEPTH = 2

N_MIXERS = 2
HEAD_DIM = 64
N_HEADS = D_MODEL // HEAD_DIM
SWA_KV_HEADS = 8
SWA_GROUP = N_HEADS // SWA_KV_HEADS
WINDOW = 128
BLOCK = 128
ROPE_THETA = 500000.0
ROT_DIM = HEAD_DIM // 4
D_FF = int(math.ceil((8 * D_MODEL / 3) / 256) * 256)
N_SWA = (DEPTH + 1) // 2
N_FOX = DEPTH // 2
RMS_EPS = 1e-6

kernel_name = "hybrid_swa_sink_fox_swiglu_sandwich"

def rmsnorm(x, g):
    x32 = x.astype(jnp.float32)
    y = x32 * lax.rsqrt(jnp.mean(x32 * x32, axis=-1, keepdims=True) + RMS_EPS) * g.astype(jnp.float32)
    return y.astype(x.dtype)

def rotary_tables(positions, dtype):
    inv_freq = ROPE_THETA ** (-jnp.arange(0, ROT_DIM, 2, dtype=jnp.float32) / ROT_DIM)
    ang = positions.astype(jnp.float32)[..., None] * inv_freq
    return jnp.cos(ang)[:, :, None, :].astype(dtype), jnp.sin(ang)[:, :, None, :].astype(dtype)

def partial_rotary(x, cos, sin):
    xr, xp = x[..., :ROT_DIM], x[..., ROT_DIM:]
    x1, x2 = xr[..., :ROT_DIM // 2], xr[..., ROT_DIM // 2:]
    rot = jnp.concatenate([x1 * cos - x2 * sin, x2 * cos + x1 * sin], axis=-1)
    return jnp.concatenate([rot, xp], axis=-1)

def swa_sink_attention(h, w_in, sinks, w_out, cos, sin):
    B, S, _ = h.shape
    nblk = S // BLOCK
    qkv = h @ w_in
    qd, kd = N_HEADS * HEAD_DIM, SWA_KV_HEADS * HEAD_DIM
    q = qkv[..., :qd].reshape(B, S, N_HEADS, HEAD_DIM)
    k = qkv[..., qd:qd + kd].reshape(B, S, SWA_KV_HEADS, HEAD_DIM)
    v = qkv[..., qd + kd:].reshape(B, S, SWA_KV_HEADS, HEAD_DIM)
    q = partial_rotary(q, cos, sin)
    k = partial_rotary(k, cos, sin)

    qb = q.reshape(B, nblk, BLOCK, SWA_KV_HEADS, SWA_GROUP, HEAD_DIM)

    def band(t):
        tb = t.reshape(B, nblk, BLOCK, SWA_KV_HEADS, HEAD_DIM)
        prev = jnp.pad(tb[:, :-1], ((0, 0), (1, 0), (0, 0), (0, 0), (0, 0)))
        return jnp.concatenate([prev, tb], axis=2)

    kband, vband = band(k), band(v)
    scale = HEAD_DIM ** -0.5
    s = jnp.einsum('bnqkgd,bnskd->bnkgqs', qb, kband).astype(jnp.float32) * scale

    q_loc = jnp.arange(BLOCK)[:, None]
    s_loc = jnp.arange(2 * BLOCK)[None, :]
    rel = BLOCK + q_loc - s_loc
    in_win = (rel >= 0) & (rel < WINDOW)
    has_prev = (jnp.arange(nblk) > 0)[:, None, None] | (s_loc >= BLOCK)[None]
    valid = (in_win[None] & has_prev)[None, :, None, None]
    s = jnp.where(valid, s, -jnp.inf)

    sink = sinks.astype(jnp.float32).reshape(SWA_KV_HEADS, SWA_GROUP)[None, None, :, :, None, None]
    m = jnp.maximum(jnp.max(s, axis=-1, keepdims=True), sink)
    p = jnp.exp(s - m)
    denom = jnp.sum(p, axis=-1, keepdims=True) + jnp.exp(sink - m)
    probs = (p / denom).astype(v.dtype)
    out = jnp.einsum('bnkgqs,bnskd->bnqkgd', probs, vband).reshape(B, S, N_HEADS * HEAD_DIM)
    return out @ w_out

def forgetting_attention(h, w_in, b_f, w_out):
    B, S, _ = h.shape
    nblk = S // BLOCK
    hd = N_HEADS * HEAD_DIM
    proj = h @ w_in
    q = proj[..., :hd].reshape(B, S, N_HEADS, HEAD_DIM)
    k = proj[..., hd:2 * hd].reshape(B, S, N_HEADS, HEAD_DIM)
    v = proj[..., 2 * hd:3 * hd].reshape(B, S, N_HEADS, HEAD_DIM)
    f_logit = proj[..., 3 * hd:]
    log_f = jax.nn.log_sigmoid(f_logit.astype(jnp.float32) + b_f.astype(jnp.float32))
    c = jnp.transpose(jnp.cumsum(log_f, axis=1), (0, 2, 1))
    key_pos = jnp.arange(S)
    scale = HEAD_DIM ** -0.5

    def block(i):
        start = i * BLOCK
        qi = lax.dynamic_slice_in_dim(q, start, BLOCK, axis=1)
        ci = lax.dynamic_slice_in_dim(c, start, BLOCK, axis=2)
        s = jnp.einsum('bqhd,bshd->bhqs', qi, k).astype(jnp.float32) * scale
        s = s + ci[..., :, None] - c[:, :, None, :]
        t_pos = start + jnp.arange(BLOCK)
        s = jnp.where(key_pos[None, :] <= t_pos[:, None], s, -jnp.inf)
        p = jax.nn.softmax(s, axis=-1).astype(v.dtype)
        return jnp.einsum('bhqs,bshd->bqhd', p, v)

    out = lax.map(block, jnp.arange(nblk))
    out = jnp.transpose(out, (1, 0, 2, 3, 4)).reshape(B, S, hd)
    return out @ w_out

def swiglu_ffn(h, w_gate_up, w_down):
    gu = h @ w_gate_up
    gate, up = gu[..., :D_FF], gu[..., D_FF:]
    return (jax.nn.silu(gate) * up) @ w_down

def setup_inputs(seed: int = 0) -> dict:
    key = jax.random.key(seed)
    ks = jax.random.split(key, 10)
    f32 = jnp.float32
    x = jax.random.normal(ks[0], (BATCH, SEQ, D_MODEL), f32)
    positions = jnp.broadcast_to(jnp.arange(SEQ, dtype=jnp.int32), (BATCH, SEQ)).astype(jnp.int32)
    norm_gains = 1.0 + 0.05 * jax.random.normal(ks[1], (DEPTH, 4, D_MODEL), f32)
    swa_in_dim = (N_HEADS + 2 * SWA_KV_HEADS) * HEAD_DIM
    swa_w_in = jax.random.normal(ks[2], (N_SWA, D_MODEL, swa_in_dim), f32) * D_MODEL ** -0.5
    swa_sinks = 0.5 * jax.random.normal(ks[3], (N_SWA, N_HEADS), f32)
    swa_w_out = jax.random.normal(ks[4], (N_SWA, N_HEADS * HEAD_DIM, D_MODEL), f32) * (N_HEADS * HEAD_DIM) ** -0.5
    fox_in_dim = 3 * N_HEADS * HEAD_DIM + N_HEADS
    fox_w_in = jax.random.normal(ks[5], (N_FOX, D_MODEL, fox_in_dim), f32) * D_MODEL ** -0.5
    fox_b_f = 2.0 + 0.5 * jax.random.normal(ks[6], (N_FOX, N_HEADS), f32)
    fox_w_out = jax.random.normal(ks[7], (N_FOX, N_HEADS * HEAD_DIM, D_MODEL), f32) * (N_HEADS * HEAD_DIM) ** -0.5
    ffn_w_gate_up = jax.random.normal(ks[8], (DEPTH, D_MODEL, 2 * D_FF), f32) * D_MODEL ** -0.5
    ffn_w_down = jax.random.normal(ks[9], (DEPTH, D_FF, D_MODEL), f32) * D_FF ** -0.5
    return {"x": x, "positions": positions, "norm_gains": norm_gains,
            "swa_w_in": swa_w_in, "swa_sinks": swa_sinks, "swa_w_out": swa_w_out,
            "fox_w_in": fox_w_in, "fox_b_f": fox_b_f, "fox_w_out": fox_w_out,
            "ffn_w_gate_up": ffn_w_gate_up, "ffn_w_down": ffn_w_down}

def reference(x, positions, norm_gains, swa_w_in, swa_sinks, swa_w_out,
              fox_w_in, fox_b_f, fox_w_out, ffn_w_gate_up, ffn_w_down):
    cos, sin = rotary_tables(positions, x.dtype)
    for i in range(DEPTH):
        g = norm_gains[i]
        h = rmsnorm(x, g[0])
        if i % N_MIXERS == 0:
            j = i // N_MIXERS
            y = swa_sink_attention(h, swa_w_in[j], swa_sinks[j], swa_w_out[j], cos, sin)
        else:
            j = i // N_MIXERS
            y = forgetting_attention(h, fox_w_in[j], fox_b_f[j], fox_w_out[j])
        x = x + rmsnorm(y, g[1])
        h = rmsnorm(x, g[2])
        y = swiglu_ffn(h, ffn_w_gate_up[i], ffn_w_down[i])
        x = x + rmsnorm(y, g[3])
    return x


_drawn_inputs = setup_inputs


def setup_inputs(seed=0):
    import zlib

    import numpy as np

    out = dict(_drawn_inputs(seed))
    spreads = {}
    factors = {}
    for name, (base, spread) in spreads.items():
        noise = np.random.default_rng([zlib.crc32(name.encode()), seed]).standard_normal(out[name].shape)
        drawn = base * np.exp(spread * noise) if base else spread * noise
        out[name] = __import__('jax').numpy.asarray(drawn.astype(out[name].dtype))
    for name, factor in factors.items():
        out[name] = (out[name] * factor).astype(out[name].dtype)
    return out
```

```python
from contextlib import ExitStack, nullcontext

import concourse.bass as bass
import numpy as np
from concourse import mybir
from concourse.alu_op_type import AluOpType as ALU

F32 = mybir.dt.float32
F32R = mybir.dt.float32r
I32 = mybir.dt.int32
ACT = mybir.ActivationFunctionType
AX = mybir.AxisListType

P = 128
D = 2048
SEQ = 256
NT = SEQ // P
KT = D // P
CH = 512
NC_D = D // CH
DH = 64
NH = D // DH
GH = CH // DH
NG = NH // GH
KV = 8
D_FF = 5632
FG = D_FF // CH
ROT = DH // 4
HALF = ROT // 2
EPS = 1e-6
SCALE = DH ** -0.5
THETA = 500000.0
NEG = -1.0e30
LOWEST = -3.0e38

UT = 16
STEPS = NT * UT
RING = 24
STAGE = 8
PAIR = 2
NSTAGE = STAGE // PAIR
LOOP_UNITS = 3
LT = LOOP_UNITS * UT

SWA_UNITS = 2 + NG
FOX_UNITS = 3 * NG
U_SWA = 0
U_SWA_OUT = U_SWA + SWA_UNITS
U_FFN = [U_SWA_OUT + NC_D, 0]
U_FOX = U_FFN[0] + 3 * FG
U_FOX_OUT = U_FOX + FOX_UNITS
U_FFN[1] = U_FOX_OUT + NC_D
U_END = U_FFN[1] + 3 * FG

STD = dict(tr=4, first=6, pt=4, pv=6, o0=21, o1=31)
LAST = dict(tr=2, first=3, pt=3, pv=5, o0=18, o1=23)


def step_order(s, last=False):
    if not last:
        return s // UT, s % UT
    if s < 24:
        return s // 12, s % 12
    return (s - 24) // 4, 12 + s % 4


def transposes_in_order():
    number = {}

    def use(*key):
        number[key] = len(number)

    for u in range(SWA_UNITS + 1):
        if u in (1, 3, 4, 5, 6):
            use("qk", {1: 0}.get(u, u - 1), 1)
        if u >= 3:
            use("o", u - 3, 0)
        if u in (0, 2, 3, 4, 5):
            use("qk", u, 0)
        if u >= 3:
            use("o", u - 3, 1)
    for c in range(NG + 1):
        u = U_FOX + 3 * c
        if c > 0:
            use("qk", u - 1, 1)
            use("o", NG + c - 1, 0)
        if c < NG:
            use("qk", u, 0)
        if c > 0:
            use("o", NG + c - 1, 1)
        if c < NG:
            use("qk", u, 1)
            use("qk", u + 2, 0)
    return number


TR = transposes_in_order()
TR_LOOP = TR[("qk", U_FOX + 6, 0)] - TR[("qk", U_FOX + 3, 0)]


def build(nc, x, positions, norm_gains, swa_w_in, swa_sinks, swa_w_out,
          fox_w_in, fox_b_f, fox_w_out, ffn_w_gate_up, ffn_w_down, out):
    with ExitStack() as ctx:
        def sb(name, shape, dt=F32):
            return ctx.enter_context(nc.sbuf_tensor(name, shape, dt))

        def sem(name):
            return ctx.enter_context(nc.semaphore(name))

        ring_hi = sb("ring_hi", [P, RING, CH], F32R)
        ring_lo = sb("ring_lo", [P, RING, CH], F32R)
        stage = sb("stage", [P, STAGE, CH])
        x_sb = sb("x_sb", [P, NT, D])
        a_hi = sb("a_hi", [P, KT, SEQ], F32R)
        a_lo = sb("a_lo", [P, KT, SEQ], F32R)
        ident = sb("ident", [P, P])
        mask = sb("mask", [P, 3, P])
        g_t = sb("g_t", [P, 2 * 4 * KT])
        rope_c = sb("rope_c", [P, NT, ROT])
        rope_s = sb("rope_s", [P, NT, ROT])
        sinks = sb("sinks", [P, NH])
        b_f = sb("b_f", [P, NH])
        ones = sb("ones", [P, 1])
        inv_freq = sb("inv_freq", [P, HALF])
        half_pow = sb("half_pow", [P, 1])
        pos_i = sb("pos_i", [P, NT], I32)
        pos_f = sb("pos_f", [P, NT])
        ssq = sb("ssq", [P, NT, NC_D])
        xsq = sb("xsq", [P, NT, NC_D])
        post_ms = sb("post_ms", [P, NT])
        post_r = sb("post_r", [P, NT])
        pre_ms = sb("pre_ms", [P, NT])
        pre_r = sb("pre_r", [P, NT])
        carrier = sb("carrier", [P, 1])
        row_mx = sb("row_mx", [P, GH, NT])
        neg_mx = sb("neg_mx", [P, GH, NT])
        den = sb("den", [P, GH, NT])
        sink_e = sb("sink_e", [P, GH, NT])
        den_all = sb("den_all", [P, GH, NT])
        rden = sb("rden", [P, GH, NT])

        KB = 1024
        arena = sb("arena", [P, 44544 // 4 - 64])
        base = arena.manual_sbuf_range[0] if arena.manual_sbuf_range else nc.lookup_mloc(arena).addr
        base = (base + 31) // 32 * 32

        def at(name, offset, shape, dt=F32):
            return nc.alloc_sbuf_tensor_at(name, shape, dt, offset=base + offset)

        o_t = at("o_t", 0, [P, KT, SEQ])
        stg = at("stg", 16 * KB, [P, NT, CH])
        v_sb = at("v_sb", 20 * KB, [P, NT, CH])
        k_t = at("k_t", 24 * KB, [P, GH // 2, SEQ])
        q_t = at("q_t", 28 * KB, [P, GH // 2, SEQ])
        prob = at("prob", 32 * KB, [P, 3, 3 * P])
        prob_t = at("prob_t", 36 * KB + 512, [P, 2, 3 * P])
        o_sb = at("o_sb", 39 * KB + 512, [P, NT, CH // 2])
        cum_b = at("cum_b", 41 * KB + 512, [P, 2, SEQ])
        y_sb = at("y_sb", 16 * KB, [P, NT, D])
        g_b = at("g_b", 32 * KB, [P, D])
        h_hi = at("h_hi", 0, [P, 4, SEQ], F32R)
        h_lo = at("h_lo", 4 * KB, [P, 4, SEQ], F32R)
        h_sb = at("h_sb", 8 * KB, [P, NT, CH])
        fg_raw = at("fg_raw", 0, [P, KT, NH])
        fg_hi = at("fg_hi", 2 * KB, [P, KT, NH], F32R)
        fg_lo = at("fg_lo", 4 * KB, [P, KT, NH], F32R)
        tri = at("tri", 6 * KB, [P, P])
        fz = at("fz", 7 * KB, [P, 6, NT, NH])
        cum_t = at("cum_t", 9 * KB, [NH, SEQ])
        rope_tmp = at("rope_tmp", 41 * KB + 512, [P, GH, ROT])
        gains_in = at("gains_in", 0, [P, P])
        trig = at("trig", 1 * KB, [P, 8, NT, HALF])

        bank = [ctx.enter_context(nc.psum_tensor(f"bank{b}", [P, CH], F32)) for b in range(8)]
        main = bank[0:4]
        o_ps, tr_ps = bank[2], bank[3]
        s_ps = bank[4:6]
        xt_ps = bank[6:8]

        x_loaded = [sem(f"x_loaded{t}") for t in range(NT)]
        gains_loaded, pos_loaded, sinks_loaded, bf_loaded = (sem(n) for n in ("gains_loaded", "pos_loaded", "sinks_loaded", "bf_loaded"))
        consts_made, gains_tr, gains_made, trig_step, rope_made = (sem(n) for n in ("consts_made", "gains_tr", "gains_made", "trig_step", "rope_made"))
        rope_part = sem("rope_part")
        raw_loaded = [sem(f"raw_loaded{k}") for k in range(NSTAGE)]
        hi_ready, lo_ready, tile_used = sem("hi_ready"), sem("lo_ready"), sem("tile_used")
        proj_done, proj_read, roped = sem("proj_done"), sem("proj_read"), sem("roped")
        tr_done, tr_read = sem("tr_done"), sem("tr_read")
        scored, row_maxed, maxed, exped = sem("scored"), sem("row_maxed"), sem("maxed"), sem("exped")
        pt_done, pt_read, pv_done = sem("pt_done"), sem("pt_read"), sem("pv_done")
        sink_diff, sink_exp, den_added, den_inverted, o_normed = (sem(n) for n in ("sink_diff", "sink_exp", "den_added", "den_inverted", "o_normed"))
        ot_hi, ot_lo = sem("ot_hi"), sem("ot_lo")
        gate_done, gate_read, up_done, hidden = sem("gate_done"), sem("gate_read"), sem("up_done"), sem("hidden")
        ht_done, ht_hi, ht_lo = sem("ht_done"), sem("ht_hi"), sem("ht_lo")
        down_done, y_added, y_squared = sem("down_done"), sem("y_added"), sem("y_squared")
        gb_loaded, post_sum, post_mean, post_rstd = sem("gb_loaded"), sem("post_sum"), sem("post_mean"), sem("post_rstd")
        y_normed, x_new = sem("y_normed"), sem("x_new")
        x_squared, pre_sum, pre_mean, pre_rstd = sem("x_squared"), sem("pre_sum"), sem("pre_mean"), sem("pre_rstd")
        xt_done, xt_hi, xt_lo = sem("xt_done"), sem("xt_hi"), sem("xt_lo")
        fg_loaded, fg_hi_made, fg_lo_made, fg_done = sem("fg_loaded"), sem("fg_hi_made"), sem("fg_lo_made"), sem("fg_done")
        fz_dve, fz_act, tri_made, cum_done, cum_made, cum_stored = (sem(n) for n in ("fz_dve", "fz_act", "tri_made", "cum_done", "cum_made", "cum_stored"))
        cum_loaded = [sem(f"cum_loaded{k}") for k in range(2)]
        biased, stored = sem("biased"), sem("stored")

        cum_dram = nc.dram_tensor("cum_scratch", (NH, SEQ), F32, kind="Internal").ap()

        def weights(u, i, pr):
            def cols(w, first, row=0):
                return w[row + pr * PAIR * P:row + (pr + 1) * PAIR * P, bass.ds(first, CH)].rearrange("(k p) n -> p k n", p=P)

            if u < U_SWA_OUT:
                c = u - U_SWA
                return cols(swa_w_in[0], D + CH * c if c < 2 else CH * (c - 2))
            if u < U_FFN[0]:
                return cols(swa_w_out[0], CH * (u - U_SWA_OUT))
            if u < U_FOX or u >= U_FFN[1]:
                layer = 0 if u < U_FOX else 1
                g, part = divmod(u - U_FFN[layer], 3)
                g = g + i
                if part < 2:
                    return cols(ffn_w_gate_up[layer], g * CH + part * D_FF)
                n, k = divmod(pr, 2)
                return ffn_w_down[layer][bass.ds(g * CH + k * PAIR * P, PAIR * P), n * CH:(n + 1) * CH].rearrange(
                    "(k p) n -> p k n", p=P)
            if u < U_FOX_OUT:
                c, part = divmod(u - U_FOX, 3)
                return cols(fox_w_in[0], c * CH + (D, 2 * D, 0)[part] + i * CH)
            return cols(fox_w_out[0], CH * (u - U_FOX_OUT))

        def gain_row(u):
            if u < U_SWA_OUT:
                return 0
            if U_FOX <= u < U_FOX_OUT:
                return 4
            for layer in range(2):
                if U_FFN[layer] <= u < U_FFN[layer] + 3 * FG and (u - U_FFN[layer]) % 3 < 2:
                    return 4 * layer + 2
            return None

        def mixer_unit(u):
            return u - U_SWA if u < U_FFN[0] else SWA_UNITS + NC_D + u - U_FOX

        def stg_before(u, t):
            if u < U_FOX:
                return None if u == 0 else TR[("qk", 0 if u == 2 else u - 1, t)]
            return TR[("qk", 5, t)] if u == U_FOX else TR[("qk", u - (1 if (u - U_FOX) % 3 == 0 else 2), t)]

        def tok(t):
            return slice(t * P, (t + 1) * P)

        def col(n):
            return slice(n * CH, (n + 1) * CH)

        def whole_program(loop, unit):
            def looped(u, n):
                with loop(n) as i:
                    for part in range(LOOP_UNITS):
                        unit(u + part, i)

            def straight(first, last):
                for u in range(first, last):
                    unit(u, 0)

            straight(U_SWA, U_FFN[0] + 3)
            looped(U_FFN[0] + 3, FG - 2)
            straight(U_FOX - 3, U_FOX + 3)
            looped(U_FOX + 3, NG - 2)
            straight(U_FOX_OUT - 3, U_FFN[1] + 3)
            looped(U_FFN[1] + 3, FG - 2)
            straight(U_END - 3, U_END)

        def ffn_part(u):
            for layer in range(2):
                if U_FFN[layer] <= u < U_FFN[layer] + 3 * FG:
                    return (layer, *divmod(u - U_FFN[layer], 3))
            return None

        def attended(u):
            if 3 <= u <= 6:
                return u - 3
            if U_FOX + 3 <= u <= U_FOX_OUT and (u - U_FOX) % 3 == 0:
                return NG + (u - U_FOX) // 3 - 1
            return None

        def holds_qk(u):
            return u in (0, 2, 3, 4, 5) or (U_FOX <= u < U_FOX_OUT and (u - U_FOX) % 3 != 1)

        def is_v(u):
            return u == 1 or (U_FOX <= u < U_FOX_OUT and (u - U_FOX) % 3 == 1)

        def out_chunk(u):
            if U_SWA_OUT <= u < U_FFN[0]:
                return u - U_SWA_OUT
            if U_FOX_OUT <= u < U_FFN[1]:
                return u - U_FOX_OUT
            return None

        def wait_swept(eng, u, i, t, n=0):
            ffn = ffn_part(u)
            if t == 1:
                eng.wait_ge(tile_used, UT * u + (4 * (n + 1) if ffn and ffn[2] == 2 else UT) + LT * i)
            elif ffn is None:
                eng.wait_ge(proj_done, mixer_unit(u) + 1 + LOOP_UNITS * i)
            elif ffn[2] < 2:
                eng.wait_ge((gate_done, up_done)[ffn[2]], ffn[0] * FG + ffn[1] + 1 + i)
            else:
                eng.wait_ge(down_done, NC_D * (ffn[0] * FG + ffn[1]) + n + 1 + NC_D * i)

        ENDS = {U_FFN[0] - 1: 1, U_FOX - 1: 2, U_FFN[1] - 1: 3, U_END - 1: 4}

        block = ctx.enter_context(nc.Block())

        @block.sync
        def _(sp):
            def unit(u, i):
                for pr in range(UT // PAIR):
                    pair = u * (UT // PAIR) + pr
                    slot = pair % NSTAGE
                    if pair >= NSTAGE:
                        sp.wait_ge(raw_loaded[slot], 16)
                        sp.wait_ge(lo_ready, PAIR * (pair - NSTAGE + 1) + LT * i)
                    sp.dma_start(stage[:, slot * PAIR:(slot + 1) * PAIR, :], weights(u, i, pr)).then_inc(raw_loaded[slot], 16)

            whole_program(lambda n: sp.Fori(0, n), unit)
            for t in range(NT):
                for q in range(NC_D):
                    sp.wait_ge(x_new, 8 * 3 + 4 * t + q + 1)
                    sp.dma_start(out[0, tok(t), col(q)], x_sb[:, t, col(q)]).then_inc(stored, 16)
            sp.wait_ge(stored, 16 * NT * NC_D)

        @block.scalar
        def _(act):
            for t in range(NT):
                act.dma_start(x_sb[:, t, :], x[0, tok(t), :]).then_inc(x_loaded[t], 16)

            def round_tile(u, i, j):
                n = u * UT + j
                pair = n // PAIR
                if j % PAIR == 0:
                    act.wait_ge(raw_loaded[pair % NSTAGE], 16 * (pair // NSTAGE + 1) + 16 * LT // STAGE * i)
                if n >= RING:
                    act.wait_ge(tile_used, n - RING + 1 + LT * i)
                row = gain_row(u)
                src = stage[:, n % STAGE, :]
                if row is None:
                    nc.scalar.activation(ring_hi[:, n % RING, :], src, ACT.Identity).then_inc(hi_ready, 1)
                else:
                    nc.scalar.activation(ring_hi[:, n % RING, :], src, ACT.Identity,
                                         scale=g_t[:, row * KT + j:row * KT + j + 1]).then_inc(hi_ready, 1)

            def x_heads(b, t, q):
                n = 8 * b + 4 * t + q
                act.wait_ge(xt_done, n + 1)
                nc.scalar.activation(a_hi[:, 4 * q:4 * q + 4, tok(t)],
                                     xt_ps[q % 2][:, :].rearrange("p (k m) -> p k m", k=4), ACT.Identity).then_inc(xt_hi, 1)
                nc.scalar.activation(y_sb[:, t, col(q)], x_sb[:, t, col(q)], ACT.Square,
                                     accum_out=xsq[:, t, q:q + 1]).then_inc(x_squared, 1)

            def read_projection(u, i, t):
                wait_swept(act, u, i, t)
                n = out_chunk(u)
                if n is not None:
                    nc.scalar.activation(y_sb[:, t, col(n)], main[t][:, :], ACT.Identity)
                    nc.scalar.activation(main[t][:, :], main[t][:, :], ACT.Square,
                                         accum_out=ssq[:, t, n:n + 1]).then_inc(proj_read, 1)
                    return
                act.wait_ge(pre_rstd, (0 if u < U_FOX else 4) + t + 1)
                if is_v(u):
                    if u > U_FOX + 1:
                        act.wait_ge(pv_done, 2 * (NG + (u - U_FOX) // 3) + 2 * i)
                    dst = v_sb[:, t, :]
                else:
                    before = stg_before(u, t)
                    if before is not None:
                        act.wait_ge(tr_done, before + 1 + TR_LOOP * i)
                    dst = stg[:, t, :]
                src = main[t][:, :]
                if 0 < u < U_FOX and not is_v(u):
                    dst = dst.rearrange("p (h a d) -> p a h d", a=2, d=DH)
                    src = src.rearrange("p (a h d) -> p a h d", a=2, d=DH)
                nc.scalar.activation(dst, src, ACT.Identity, scale=pre_r[:, t:t + 1]).then_inc(proj_read, 1)

            def exponentials(G, i, j):
                n = GH * G + j
                act.wait_ge(maxed, n + 1 + GH * i)
                b = j % 3
                nc.scalar.activation(prob[:, b, 0:P], prob[:, b, 0:P], ACT.Exp, bias=neg_mx[:, j, 0:1],
                                     accum_out=den[:, j, 0:1])
                nc.scalar.activation(prob[:, b, P:3 * P], prob[:, b, P:3 * P], ACT.Exp, bias=neg_mx[:, j, 1:2],
                                     accum_out=den[:, j, 1:2]).then_inc(exped, 1)

            def sink_terms(G, g4):
                if G < NG:
                    act.wait_ge(sink_diff, 2 * G + g4 + 1)
                    nc.scalar.activation(sink_e[:, 4 * g4:4 * g4 + 4, :], sink_e[:, 4 * g4:4 * g4 + 4, :],
                                         ACT.Exp).then_inc(sink_exp, 1)

            def o_heads(layer, kp):
                G, g4 = divmod(kp, 2)
                act.wait_ge(tr_read, TR[("o", NG * layer + G, g4)] + 1)
                nc.scalar.activation(a_hi[:, 2 * kp:2 * kp + 2, :], o_t[:, 2 * kp:2 * kp + 2, :],
                                     ACT.Identity).then_inc(ot_hi, 1)

            def forget_gate(s):
                if s == 17:
                    act.wait_ge(fg_loaded, 16)
                    for k in range(KT):
                        nc.scalar.activation(fg_hi[:, k, :], fg_raw[:, k, :], ACT.Identity,
                                             scale=g_t[:, 4 * KT + k:4 * KT + k + 1]).then_inc(fg_hi_made, 1)
                if s == 27:
                    act.wait_ge(fz_dve, 2)
                    nc.scalar.activation(fz[:, 2], fz[:, 1], ACT.Exp).then_inc(fz_act, 1)
                    act.wait_ge(fz_act, 1)
                    nc.scalar.activation(fz[:, 3], fz[:, 2], ACT.Ln, bias=1.0).then_inc(fz_act, 1)

            def unit(u, i):
                ffn = ffn_part(u)
                G = attended(u)
                when = LAST if u in (U_SWA_OUT, U_FOX_OUT) else STD
                first_of_ffn = ffn and ffn[1:] == (0, 0)
                for s in range(STEPS):
                    if s == 0 and u > 0 and ffn_part(u - 1) is None:
                        read_projection(u - 1, i, 1)
                    if s % 2 == 0 and u + 1 < U_END:
                        round_tile(u + 1, i, s // 2)
                    if ffn is None:
                        if u in (U_SWA_OUT, U_FOX_OUT):
                            if s == 0:
                                for kp in range(6):
                                    o_heads(0 if u < U_FOX else 1, kp)
                            if s == 20:
                                o_heads(0 if u < U_FOX else 1, 6)
                            if s == 24:
                                o_heads(0 if u < U_FOX else 1, 7)
                            if s == 28:
                                read_projection(u, i, 0)
                        elif s == 16:
                            read_projection(u, i, 0)
                        if u == U_FOX:
                            forget_gate(s)
                    if G is not None:
                        j, odd = divmod(s - when["first"] - 1, 2)
                        if odd == 0 and 0 <= j < GH:
                            exponentials(G, i, j)
                        j, odd = divmod(s - when["first"] - when["pv"], 2)
                        if odd == 0 and j in (3, 7):
                            sink_terms(G, j // 4)
                    if ffn:
                        layer, g, part = ffn
                        f = layer * FG + g
                        if part == 1 and s in (0, 2):
                            t = s // 2
                            wait_swept(act, u - 1, i, t)
                            act.wait_ge(pre_rstd, 2 * (2 * layer + 1) + t + 1)
                            if g > 0:
                                act.wait_ge(ht_done, 2 * (f - 1) + t + 1 + 2 * i)
                            nc.scalar.activation(h_sb[:, t, :], main[t][:, :], ACT.Silu,
                                                 scale=pre_r[:, t:t + 1]).then_inc(gate_read, 1)
                        if (part, s) in ((1, 21), (2, 5)):
                            t = 0 if part == 1 else 1
                            act.wait_ge(ht_done, 2 * f + t + 1 + 2 * i)
                            nc.scalar.activation(h_hi[:, :, tok(t)], xt_ps[t][:, :].rearrange("p (k m) -> p k m", k=4),
                                                 ACT.Identity).then_inc(ht_hi, 1)
                    if u in ENDS:
                        b = ENDS[u]
                        if b in (2, 4) and s in (5, 9, 13, 17):
                            squares_of_y(b, 0, (s - 5) // 4)
                        if b < 4 and s in (22, 25, 28, 31):
                            x_heads(b, 0, (s - 22) // 3)
                    if u - 1 in ENDS:
                        b = ENDS[u - 1]
                        if b == 2 and s in (0, 1, 2, 3):
                            squares_of_y(b, 1, s)
                        if s in (8, 10, 12, 14):
                            x_heads(b, 1, (s - 8) // 2)

            def squares_of_y(b, t, n):
                f = (b // 2) * FG - 1
                act.wait_ge(y_added, 8 * f + 4 * t + n + 1)
                nc.scalar.activation(main[n][:, :], y_sb[:, t, col(n)], ACT.Square,
                                     accum_out=ssq[:, t, n:n + 1]).then_inc(y_squared, 1)

            act.wait_ge(gains_made, 1)
            for j in range(4):
                round_tile(0, 0, j)
            for t in range(NT):
                for q in range(NC_D):
                    x_heads(0, t, q)
                    for j in range(4 + 6 * t + 3 * q // 2, 4 + 6 * t + 3 * (q + 1) // 2):
                        round_tile(0, 0, j)
            act.wait_ge(trig_step, 10)
            nc.scalar.activation(trig[:, 6], trig[:, 4], ACT.Sin)
            nc.scalar.activation(trig[:, 7], trig[:, 5], ACT.Sin).then_inc(rope_made, 1)
            whole_program(lambda n: act.Fori(0, n), unit)
            for n in range(NC_D):
                squares_of_y(4, 1, n)

        @block.vector
        def _(dve):
            def rest_tile(u, i, j):
                n = u * UT + j
                dve.wait_ge(hi_ready, n + 1 + LT * i)
                row = gain_row(u)
                src, hi, lo = stage[:, n % STAGE, :], ring_hi[:, n % RING, :].bitcast(F32), ring_lo[:, n % RING, :]
                if row is None:
                    nc.vector.tensor_tensor(lo, src, hi, ALU.subtract).then_inc(lo_ready, 1)
                else:
                    nc.vector.scalar_tensor_tensor(out=lo, in0=src, scalar=g_t[:, row * KT + j:row * KT + j + 1], in1=hi,
                                                   op0=ALU.mult, op1=ALU.subtract).then_inc(lo_ready, 1)

            def x_rests(b, t, q):
                n = 8 * b + 4 * t + q
                dve.wait_ge(xt_hi, n + 1)
                hi = a_hi[:, 4 * q:4 * q + 4, tok(t)].bitcast(F32)
                nc.vector.tensor_tensor(a_lo[:, 4 * q:4 * q + 4, tok(t)], xt_ps[q % 2][:, :].rearrange("p (k m) -> p k m", k=4),
                                        hi, ALU.subtract).then_inc(xt_lo, 1)

            def mean_square(src, dst, t, summed, count, meaned):
                nc.vector.tensor_reduce(dst[:, t:t + 1], src[:, t, :], AX.X, ALU.add).then_inc(summed, 1)
                dve.wait_ge(summed, count)
                nc.vector.tensor_scalar(dst[:, t:t + 1], dst[:, t:t + 1], 1.0 / D, EPS, ALU.mult, ALU.add).then_inc(meaned, 1)

            def x_mean(b, t):
                dve.wait_ge(x_squared, 8 * b + 4 * t + 4)
                mean_square(xsq, pre_ms, t, pre_sum, 2 * b + t + 1, pre_mean)

            def y_mean(b, t):
                if b % 2:
                    dve.wait_ge(proj_read, 2 * mixer_unit((U_FFN[0] if b == 1 else U_FFN[1]) - 1) + t + 1)
                else:
                    dve.wait_ge(y_squared, 8 * (b // 2 - 1) + 4 * t + 4)
                mean_square(ssq, post_ms, t, post_sum, 2 * (b - 1) + t + 1, post_mean)

            def y_norm(b, t, q):
                if q == 0:
                    dve.wait_ge(post_rstd, 2 * (b - 1) + t + 1)
                    dve.wait_ge(gb_loaded, 16 * b)
                nc.vector.scalar_tensor_tensor(out=y_sb[:, t, col(q)], in0=y_sb[:, t, col(q)], scalar=post_r[:, t:t + 1],
                                               in1=g_b[:, col(q)], op0=ALU.mult, op1=ALU.mult).then_inc(y_normed, 1)

            def read_transposed(u, i, t):
                n = TR[("qk", u, t)]
                dve.wait_ge(tr_done, n + 1 + TR_LOOP * i)
                is_k = u in (0, U_FOX) or (u > U_FOX and (u - U_FOX) % 3 == 0)
                dst = k_t if is_k else q_t
                nc.vector.tensor_copy(dst[:, :, tok(t)], tr_ps[:, :].rearrange("p (k m) -> p k m", k=GH // 2)).then_inc(tr_read, 1)

            def read_output(G, i, g4):
                n = TR[("o", G, g4)]
                dve.wait_ge(tr_done, n + 1 + TR_LOOP * i)
                first = 4 * (G % NG) + 2 * g4 + 4 * i
                nc.vector.tensor_copy(o_t[:, bass.ds(first, 2), :], tr_ps[:, :].rearrange("p (k m) -> p k m", k=2)).then_inc(tr_read, 1)

            def masked_max(G, i, j):
                n = GH * G + j
                dve.wait_ge(scored, n + 1 + GH * i)
                b = j % 3
                if G < NG:
                    if G > 0 or j >= 3:
                        dve.wait_ge(pt_done, n - 2 if j >= 3 else GH * G)
                    init = sinks[:, GH * G + j:GH * G + j + 1]
                    add = mask[:, :, :].rearrange("p a b -> p (a b)")
                else:
                    dve.wait_ge(biased, n - GH * NG + 1 + GH * i)
                    nc.vector.memset(carrier[:, :], 0.0)
                    init = LOWEST
                    add = prob[:, b, :]
                for t, (lo, hi) in enumerate(((0, P), (P, 3 * P))):
                    last = nc.vector.tensor_tensor_reduce(out=prob[:, b, lo:hi], in0=s_ps[j % 2][:, lo:hi], in1=add[:, lo:hi],
                                                          scale=SCALE, scalar=init, op0=ALU.add, op1=ALU.max,
                                                          accum_out=row_mx[:, j, t:t + 1])
                last.then_inc(row_maxed, 1)
                dve.wait_ge(row_maxed, n + 1 + GH * i)
                nc.vector.tensor_scalar(neg_mx[:, j, :], row_mx[:, j, :], -1.0, None, ALU.mult).then_inc(maxed, 1)

            def read_probabilities(G, i, j):
                n = GH * G + j
                dve.wait_ge(pt_done, n + 1 + GH * i)
                nc.vector.tensor_copy(prob_t[:, j % 2, :], xt_ps[j % 2][:, 0:3 * P]).then_inc(pt_read, 1)

            def sink_difference(G, g4):
                if G < NG:
                    h = GH * G + 4 * g4
                    dve.wait_ge(maxed, h + 4)
                    nc.vector.tensor_tensor(sink_e[:, 4 * g4:4 * g4 + 4, :], neg_mx[:, 4 * g4:4 * g4 + 4, :],
                                            sinks[:, h:h + 4].unsqueeze(2).to_broadcast([P, 4, NT]), ALU.add).then_inc(sink_diff, 1)

            def normalise(G, i, g4):
                n = 2 * G + g4
                part = slice(4 * g4, 4 * g4 + 4)
                dve.wait_ge(exped, GH * G + 4 * g4 + 4 + GH * i)
                if G < NG:
                    dve.wait_ge(sink_exp, n + 1)
                    nc.vector.tensor_tensor(den_all[:, part, :], den[:, part, :], sink_e[:, part, :], ALU.add).then_inc(den_added, 1)
                    dve.wait_ge(den_added, n + 1)
                    nc.vector.reciprocal(rden[:, part, :], den_all[:, part, :]).then_inc(den_inverted, 1)
                else:
                    nc.vector.reciprocal(rden[:, part, :], den[:, part, :]).then_inc(den_inverted, 1)
                dve.wait_ge(den_inverted, n + 1 + 2 * i)
                dve.wait_ge(pv_done, n + 1 + 2 * i)
                dve.wait_ge(tr_done, TR[("o", G, g4)] + TR_LOOP * i)
                nc.vector.tensor_tensor(o_sb[:, :, :].rearrange("p t (j d) -> p t j d", d=DH),
                                        o_ps[:, :].rearrange("p (t j d) -> p t j d", t=NT, d=DH),
                                        rden[:, part, :].rearrange("p j t -> p t j").unsqueeze(3).to_broadcast([P, NT, 4, DH]),
                                        ALU.mult).then_inc(o_normed, 1)

            def o_rests(layer, kp):
                dve.wait_ge(ot_hi, 8 * layer + kp + 1)
                nc.vector.tensor_tensor(a_lo[:, 2 * kp:2 * kp + 2, :], o_t[:, 2 * kp:2 * kp + 2, :],
                                        a_hi[:, 2 * kp:2 * kp + 2, :].bitcast(F32), ALU.subtract).then_inc(ot_lo, 1)

            def forget_gate(s):
                if s == 17:
                    for k in range(KT):
                        dve.wait_ge(fg_hi_made, k + 1)
                        nc.vector.scalar_tensor_tensor(out=fg_lo[:, k, :], in0=fg_raw[:, k, :],
                                                       scalar=g_t[:, 4 * KT + k:4 * KT + k + 1], in1=fg_hi[:, k, :].bitcast(F32),
                                                       op0=ALU.mult, op1=ALU.subtract).then_inc(fg_lo_made, 1)
                if s == 24:
                    dve.wait_ge(bf_loaded, 16)
                    for t in range(NT):
                        dve.wait_ge(fg_done, t + 1)
                        dve.wait_ge(pre_rstd, 2 * 2 + t + 1)
                        last = nc.vector.scalar_tensor_tensor(out=fz[:, 0, t, :], in0=s_ps[t][:, 0:NH], scalar=pre_r[:, t:t + 1],
                                                              in1=b_f[:, :], op0=ALU.mult, op1=ALU.add)
                    last.then_inc(fz_dve, 1)
                    dve.wait_ge(fz_dve, 1)
                    nc.vector.scalar_tensor_tensor(out=fz[:, 1], in0=fz[:, 0], scalar=-1.0, in1=fz[:, 0],
                                                   op0=ALU.mult, op1=ALU.min).then_inc(fz_dve, 1)
                if s == 30:
                    dve.wait_ge(fz_act, 2)
                    nc.vector.scalar_tensor_tensor(out=fz[:, 4], in0=fz[:, 0], scalar=0.0, in1=fz[:, 3],
                                                   op0=ALU.min, op1=ALU.subtract).then_inc(fz_dve, 1)

            def read_cumulated():
                dve.wait_ge(cum_done, 1)
                nc.vector.tensor_scalar(cum_t[:, :], s_ps[0][0:NH, 0:SEQ], -1.0 / SCALE, None, ALU.mult).then_inc(cum_made, 1)

            def unit(u, i):
                ffn = ffn_part(u)
                G = attended(u)
                when = LAST if u in (U_SWA_OUT, U_FOX_OUT) else STD
                for s in range(STEPS):
                    if u in ENDS:
                        b = ENDS[u]
                        if s == 19:
                            y_mean(b, 0)
                        if s in (21, 22, 23, 24):
                            y_norm(b, 0, s - 21)
                        if b < 4 and s in (23, 26, 29, 31):
                            x_rests(b, 0, (s - 22) // 3)
                    if u - 1 in ENDS:
                        b = ENDS[u - 1]
                        if s == 4:
                            x_mean(b, 0)
                            y_mean(b, 1)
                        if s in (5, 6, 7, 8):
                            y_norm(b, 1, s - 5)
                        if s in (9, 11, 13, 15):
                            x_rests(b, 1, (s - 9) // 2)
                        if s == 16:
                            x_mean(b, 1)
                    if u + 1 < U_END and s % 2 == 0:
                        rest_tile(u + 1, i, s // 2)
                    if ffn is None:
                        if holds_qk(u) and s == 24:
                            read_transposed(u, i, 0)
                        if u > 0 and holds_qk(u - 1) and s == (when["tr"] if G is not None else STD["tr"]):
                            read_transposed(u - 1, i, 1)
                        if u in (U_SWA_OUT, U_FOX_OUT):
                            layer = 0 if u < U_FOX else 1
                            if s == 0:
                                for kp in range(6):
                                    o_rests(layer, kp)
                            if s == 20:
                                o_rests(layer, 6)
                            if s == 24:
                                o_rests(layer, 7)
                        if u == U_FOX:
                            forget_gate(s)
                        if u == U_FOX + 1 and s == 4:
                            read_cumulated()
                    if G is not None:
                        j, odd = divmod(s - when["first"] - when["pt"], 2)
                        if odd == 0 and 0 <= j < GH:
                            read_probabilities(G, i, j)
                        j, odd = divmod(s - when["first"], 2)
                        if odd == 0 and 0 <= j < GH:
                            masked_max(G, i, j)
                            if j in (3, 7):
                                sink_difference(G, j // 4)
                        j, odd = divmod(s - when["first"] - when["pv"], 2)
                        if odd == 0 and j in (3, 7):
                            normalise(G, i, j // 4)
                        if s == when["o0"]:
                            read_output(G, i, 0)
                        if s == when["o1"]:
                            read_output(G, i, 1)
                    if ffn:
                        layer, g, part = ffn
                        f = layer * FG + g
                        if (part, s) in ((1, 17), (2, 1)):
                            t = 0 if part == 1 else 1
                            dve.wait_ge(gate_read, 2 * f + t + 1 + 2 * i)
                            wait_swept(dve, u if part == 1 else u - 1, i, t)
                            nc.vector.scalar_tensor_tensor(out=h_sb[:, t, :], in0=main[2 + t][:, :], scalar=pre_r[:, t:t + 1],
                                                           in1=h_sb[:, t, :], op0=ALU.mult, op1=ALU.mult).then_inc(hidden, 1)
                        if (part, s) in ((1, 22), (2, 6)):
                            t = 0 if part == 1 else 1
                            dve.wait_ge(ht_hi, 2 * f + t + 1 + 2 * i)
                            nc.vector.tensor_tensor(h_lo[:, :, tok(t)], xt_ps[t][:, :].rearrange("p (k m) -> p k m", k=4),
                                                    h_hi[:, :, tok(t)].bitcast(F32), ALU.subtract).then_inc(ht_lo, 1)
                        if part == 2 and (s % 4 == 0 and s > 0 or s == STEPS - 1):
                            add_y(u, f, i, g, (s + 1) // 4 - 1)

            def add_y(u, f, i, g, k):
                t, n = divmod(k, NC_D)
                wait_swept(dve, u, i, t, n)
                dst = y_sb[:, t, col(n)]
                if g == 0:
                    nc.vector.tensor_copy(dst, main[n][:, :]).then_inc(y_added, 1)
                else:
                    dve.wait_ge(y_added, 8 * (f - 1) + k + 1 + 8 * i)
                    nc.vector.tensor_tensor(dst, main[n][:, :], dst, ALU.add).then_inc(y_added, 1)

            dve.wait_ge(gains_tr, 1)
            nc.vector.tensor_copy(g_t[:, :], tr_ps[:, 0:P]).then_inc(gains_made, 1)
            dve.wait_ge(gains_made, 1)
            for j in range(4):
                rest_tile(0, 0, j)
            for t in range(NT):
                for q in range(NC_D):
                    x_rests(0, t, q)
                    for j in range(4 + 6 * t + 3 * q // 2, 4 + 6 * t + 3 * (q + 1) // 2):
                        rest_tile(0, 0, j)
            for t in range(NT):
                x_mean(0, t)

            chain = [0]

            def step(ins):
                chain[0] += 1
                ins.then_inc(trig_step, 1)
                dve.wait_ge(trig_step, chain[0])

            two_pi = 2 * np.pi
            c1 = 6.28125
            c2 = float(np.float32(np.floor((two_pi - c1) * 2 ** 20) / 2 ** 20))
            c3 = two_pi - c1 - c2
            magic = 1.5 * 2.0 ** 23
            dve.wait_ge(pos_loaded, 16)
            dve.wait_ge(consts_made, 1)
            step(nc.vector.tensor_copy(pos_f[:, :], pos_i[:, :]))
            for t in range(NT):
                last = nc.vector.tensor_scalar(trig[:, 0, t, :], inv_freq[:, :], pos_f[:, t:t + 1], None, ALU.mult)
            step(last)
            step(nc.vector.tensor_scalar(trig[:, 1], trig[:, 0], 1.0 / two_pi, magic, ALU.mult, ALU.add))
            step(nc.vector.tensor_scalar(trig[:, 1], trig[:, 1], magic, None, ALU.subtract))
            for c in (c1, c2, c3):
                step(nc.vector.scalar_tensor_tensor(out=trig[:, 0], in0=trig[:, 1], scalar=-c, in1=trig[:, 0], op0=ALU.mult, op1=ALU.add))
            step(nc.vector.tensor_scalar(trig[:, 4], trig[:, 0], 3.1415925, -3.1415925, ALU.min, ALU.max))
            step(nc.vector.scalar_tensor_tensor(out=trig[:, 5], in0=trig[:, 4], scalar=-1.0, in1=trig[:, 4], op0=ALU.mult, op1=ALU.min))
            step(nc.vector.tensor_scalar(trig[:, 5], trig[:, 5], float(np.pi / 2), None, ALU.add))
            dve.wait_ge(rope_made, 1)
            for h in range(2):
                part = slice(h * HALF, (h + 1) * HALF)
                nc.vector.tensor_copy(rope_c[:, :, part], trig[:, 7])
                last = nc.vector.tensor_scalar(rope_s[:, :, part], trig[:, 6], -1.0 if h == 0 else 1.0, None, ALU.mult)
            last.then_inc(rope_made, 1)
            dve.wait_ge(sinks_loaded, 16)

            whole_program(lambda n: dve.Fori(0, n), unit)
            y_mean(4, 1)
            for q in range(NC_D):
                y_norm(4, 1, q)

        @block.gpsimd
        def _(pool):
            pool.dma_start(gains_in[:, :], norm_gains.rearrange("l g (k p) -> (l g k) p", p=P)).then_inc(gains_loaded, 16)
            with nc.allow_non_contiguous_dma(reason="256 positions"):
                pool.dma_start(pos_i[:, :], positions.rearrange("b (t p) -> p (b t)", p=P)).then_inc(pos_loaded, 16)
            pool.dma_start(sinks[:, :], swa_sinks[0, :].partition_broadcast(P)).then_inc(sinks_loaded, 16)
            pool.dma_start(b_f[:, :], fox_b_f[0, :].partition_broadcast(P)).then_inc(bf_loaded, 16)
            nc.gpsimd.memset(ident[:, :], 0.0)
            nc.gpsimd.memset(mask[:, :, :], 0.0)
            nc.gpsimd.memset(ones[:, :], 1.0)
            nc.gpsimd.memset(half_pow[:, :], -0.5)
            freq = np.float32(THETA) ** (-np.arange(0, ROT, 2, dtype=np.float32) / np.float32(ROT))
            for k in range(HALF):
                last = nc.gpsimd.memset(inv_freq[:, k:k + 1], float(freq[k]))
            last.then_inc(consts_made, 1)
            pool.wait_ge(consts_made, 1)
            nc.gpsimd.affine_select(out=ident[:, :], in_=ident[:, :], compare_op=ALU.not_equal, fill=1.0, base=0,
                                    pattern=[[-1, P]], channel_multiplier=1)
            for a in (0, 2):
                nc.gpsimd.affine_select(out=mask[:, a, :], in_=mask[:, a, :], compare_op=ALU.is_ge, fill=NEG, base=0,
                                        pattern=[[-1, P]], channel_multiplier=1)
            nc.gpsimd.affine_select(out=mask[:, 1, :], in_=mask[:, 1, :], compare_op=ALU.is_gt, fill=NEG, base=0,
                                    pattern=[[1, P]], channel_multiplier=-1).then_inc(consts_made, 1)

            def rstd(src, dst, t, meaned, count, done):
                pool.wait_ge(meaned, count)
                nc.gpsimd.tensor_tensor(dst[:, t:t + 1], src[:, t:t + 1], half_pow[:, :], ALU.pow).then_inc(done, 1)

            def post(b, t):
                rstd(post_ms, post_r, t, post_mean, 2 * (b - 1) + t + 1, post_rstd)
                for q in range(NC_D):
                    pool.wait_ge(y_normed, 8 * (b - 1) + 4 * t + q + 1)
                    nc.gpsimd.tensor_tensor(x_sb[:, t, col(q)], x_sb[:, t, col(q)], y_sb[:, t, col(q)], ALU.add).then_inc(x_new, 1)

            def rope(u, t):
                r = max(u - 1, 0)
                pool.wait_ge(proj_read, 2 * u + t + 1)
                v = stg[:, t, :].rearrange("p (h d) -> p h d", d=DH)
                tmp = rope_tmp
                if 2 * r + t > 0:
                    pool.wait_ge(roped, 2 * r + t)
                c = rope_c[:, t, :].unsqueeze(1).to_broadcast([P, GH, ROT])
                s1 = rope_s[:, t, 0:HALF].unsqueeze(1).to_broadcast([P, GH, HALF])
                s2 = rope_s[:, t, HALF:ROT].unsqueeze(1).to_broadcast([P, GH, HALF])
                nc.gpsimd.tensor_tensor(tmp[:, :, 0:HALF], v[:, :, HALF:ROT], s1, ALU.mult)
                nc.gpsimd.tensor_tensor(tmp[:, :, HALF:ROT], v[:, :, 0:HALF], s2, ALU.mult).then_inc(rope_part, 1)
                n = 2 * (2 * r + t)
                pool.wait_ge(rope_part, n + 1)
                nc.gpsimd.tensor_tensor(v[:, :, 0:ROT], v[:, :, 0:ROT], c, ALU.mult).then_inc(rope_part, 1)
                pool.wait_ge(rope_part, n + 2)
                nc.gpsimd.tensor_tensor(v[:, :, 0:ROT], v[:, :, 0:ROT], tmp[:, :, :], ALU.add).then_inc(roped, 1)

            def load_cum(c, i, j):
                pool.dma_start(cum_b[:, j % 2, :], cum_dram[bass.ds(GH * c + j + GH * i, 1), :].to_broadcast([P, SEQ])).then_inc(
                    cum_loaded[j % 2], 16)

            def bias(c, i, j):
                n = GH * c + j
                pool.wait_ge(cum_loaded[j % 2], 16 * (GH // 2 * c + j // 2 + 1) + 16 * (GH // 2) * i)
                pool.wait_ge(pt_done, GH * NG + (n - 2 if j >= 3 else GH * c) + GH * i)
                cb = cum_b[:, j % 2, :]
                pb = prob[:, j % 3, :]
                nc.gpsimd.tensor_tensor(pb[:, 0:P], cb[:, 0:P], mask[:, 0, :], ALU.add)
                nc.gpsimd.tensor_copy(pb[:, P:2 * P], cb[:, 0:P])
                nc.gpsimd.tensor_tensor(pb[:, 2 * P:3 * P], cb[:, P:SEQ], mask[:, 2, :], ALU.add).then_inc(biased, 1)
                if j + 2 < GH:
                    pool.wait_ge(biased, n + 1 + GH * i)
                    load_cum(c, i, j + 2)

            def load_gains(b):
                layer, which = divmod(b - 1, 2)
                pool.dma_start(g_b[:, :], norm_gains[layer, 2 * which + 1, :].partition_broadcast(P)).then_inc(gb_loaded, 16)

            for t in range(NT):
                rstd(pre_ms, pre_r, t, pre_mean, t + 1, pre_rstd)
            pool.wait_ge(rope_made, 2)
            for u in (0, 2, 3, 4, 5):
                for t in range(NT):
                    rope(u, t)
            for layer in range(2):
                pool.wait_ge(tr_done, TR[("o", NG * layer + NG - 1, 1)] + 1)
                load_gains(2 * layer + 1)
                for b in (2 * layer + 1, 2 * layer + 2):
                    post(b, 0)
                    if b < 4:
                        rstd(pre_ms, pre_r, 0, pre_mean, 2 * b + 1, pre_rstd)
                    if b == 2:
                        pool.wait_ge(tile_used, UT * U_FOX)
                        pool.dma_start(fg_raw[:, :, :], fox_w_in[0][:, 3 * D:3 * D + NH].rearrange("(k p) n -> p k n", p=P)).then_inc(fg_loaded, 16)
                    post(b, 1)
                    if b < 4:
                        rstd(pre_ms, pre_r, 1, pre_mean, 2 * b + 2, pre_rstd)
                    if b == 2 * layer + 1:
                        load_gains(b + 1)
                if layer == 0:
                    nc.gpsimd.memset(tri[:, :], 1.0).then_inc(tri_made, 1)
                    pool.wait_ge(tri_made, 1)
                    nc.gpsimd.affine_select(out=tri[:, :], in_=tri[:, :], compare_op=ALU.is_ge, fill=0.0, base=0,
                                            pattern=[[1, P]], channel_multiplier=-1).then_inc(tri_made, 1)
                    pool.wait_ge(cum_made, 1)
                    pool.dma_start(cum_dram, cum_t[:, :]).then_inc(cum_stored, 16)
                    pool.wait_ge(cum_stored, 16)
                    pool.wait_ge(y_normed, 16)
                    with pool.Fori(0, NG) as c:
                        load_cum(0, c, 0)
                        load_cum(0, c, 1)
                        for j in range(GH):
                            bias(0, c, j)
                        pool.wait_ge(biased, GH * c + GH)

        @block.tensor
        def _(pe):
            def product(dst, hi_a, lo_a, hi_w, lo_w, start, stop):
                nc.tensor.matmul(dst, hi_a, hi_w, start=start, stop=False)
                nc.tensor.matmul(dst, hi_a, lo_w, start=False, stop=False)
                return nc.tensor.matmul(dst, lo_a, hi_w, start=False, stop=stop)

            def transpose_x(b, t, q):
                n = 8 * b + 4 * t + q
                if b == 0:
                    pe.wait_ge(x_loaded[t], 16)
                else:
                    pe.wait_ge(x_new, 8 * (b - 1) + 4 * t + q + 1)
                if n >= 2:
                    pe.wait_ge(xt_lo, n - 1)
                for k in range(4):
                    last = nc.tensor.transpose(xt_ps[q % 2][:, k * P:(k + 1) * P], x_sb[:, t, col(q)][:, k * P:(k + 1) * P], ident[:, :])
                last.then_inc(xt_done, 1)

            def free_tr(n, i):
                if n >= 1:
                    pe.wait_ge(tr_read, n + TR_LOOP * i)

            def transpose_qk(u, i, t):
                if u < U_FOX:
                    pe.wait_ge(roped, 2 * max(u - 1, 0) + t + 1)
                else:
                    pe.wait_ge(proj_read, 2 * mixer_unit(u) + t + 1 + 6 * i)
                free_tr(TR[("qk", u, t)], i)
                src = stg[:, t, :]
                for k in range(GH // 2):
                    last = nc.tensor.transpose(tr_ps[:, k * P:(k + 1) * P], src[:, k * P:(k + 1) * P], ident[:, :])
                last.then_inc(tr_done, 1)

            def transpose_o(G, i, g4):
                pe.wait_ge(o_normed, 2 * G + g4 + 1 + 2 * i)
                free_tr(TR[("o", G, g4)], i)
                for k in range(2):
                    for t in range(NT):
                        last = nc.tensor.transpose(tr_ps[:, (2 * k + t) * P:(2 * k + t + 1) * P], o_sb[:, t, k * P:(k + 1) * P], ident[:, :])
                last.then_inc(tr_done, 1)

            def where(G, j):
                if G < NG:
                    a = j // 4
                    return DH * a, j % 4, G, DH * (2 * G + a)
                return DH * (j % 2), j // 2, j // 2, DH * j

            def scores(G, i, j):
                n = GH * G + j
                if j == 0:
                    pe.wait_ge(tr_read, TR[("qk", qk_unit(G), 1)] + 1 + TR_LOOP * i)
                if n >= 2:
                    pe.wait_ge(row_maxed, n - 1 + GH * i)
                p0, a, b, _ = where(G, j)
                rows = slice(p0, p0 + DH)
                nc.tensor.matmul(s_ps[j % 2][:, 0:P], q_t[rows, a, 0:P], k_t[rows, b, 0:P], start=True, stop=True)
                nc.tensor.matmul(s_ps[j % 2][:, P:3 * P], q_t[rows, a, P:SEQ], k_t[rows, b, :], start=True, stop=True).then_inc(scored, 1)

            def transpose_p(G, i, j):
                n = GH * G + j
                pe.wait_ge(exped, n + 1 + GH * i)
                if n >= 2:
                    pe.wait_ge(pt_read, n - 1 + GH * i)
                for a in range(3):
                    last = nc.tensor.transpose(xt_ps[j % 2][:, a * P:(a + 1) * P], prob[:, j % 3, a * P:(a + 1) * P], ident[:, :])
                last.then_inc(pt_done, 1)

            def times_v(G, i, j):
                n = GH * G + j
                pe.wait_ge(pt_read, n + 1 + GH * i)
                if j % 4 == 0 and n > 0:
                    pe.wait_ge(o_normed, n // 4 + 2 * i)
                v0 = where(G, j)[3]
                dst = o_ps[:, :].rearrange("p (t j d) -> p t j d", t=NT, d=DH)
                pt = prob_t[:, j % 2, :]
                nc.tensor.matmul(dst[:, 0, j % 4], pt[:, 0:P], v_sb[:, 0, v0:v0 + DH], start=True, stop=True)
                nc.tensor.matmul(dst[:, 1, j % 4], pt[:, P:2 * P], v_sb[:, 0, v0:v0 + DH], start=True, stop=False)
                last = nc.tensor.matmul(dst[:, 1, j % 4], pt[:, 2 * P:3 * P], v_sb[:, 1, v0:v0 + DH], start=False, stop=True)
                if j % 4 == 3:
                    last.then_inc(pv_done, 1)

            def qk_unit(G):
                return 2 + G if G < NG else U_FOX + 3 * (G - NG) + 2

            def hidden_transposes(f, i, t):
                pe.wait_ge(hidden, 2 * f + t + 1 + 2 * i)
                for k in range(4):
                    last = nc.tensor.transpose(xt_ps[t][:, k * P:(k + 1) * P], h_sb[:, t, k * P:(k + 1) * P], ident[:, :])
                last.then_inc(ht_done, 1)

            def forget_gate():
                pe.wait_ge(fg_lo_made, KT)
                for t in range(NT):
                    for k in range(KT):
                        last = product(s_ps[t][:, 0:NH], a_hi[:, k, tok(t)], a_lo[:, k, tok(t)], fg_hi[:, k, :], fg_lo[:, k, :],
                                       k == 0, k == KT - 1)
                    last.then_inc(fg_done, 1)

            def cumulate():
                pe.wait_ge(fz_dve, 3)
                pe.wait_ge(tri_made, 2)
                dst = s_ps[0]
                nc.tensor.matmul(dst[0:NH, 0:P], fz[:, 4, 0, :], tri[:, :], start=True, stop=True)
                nc.tensor.matmul(dst[0:NH, P:SEQ], fz[:, 4, 0, :], ones[:, :].to_broadcast([P, P]), start=True, stop=False)
                nc.tensor.matmul(dst[0:NH, P:SEQ], fz[:, 4, 1, :], tri[:, :], start=False, stop=True).then_inc(cum_done, 1)

            def input_block(u, s, t, j, last_order):
                b = {0: 0, U_FFN[0]: 1, U_FOX: 2, U_FFN[1]: 3}.get(u)
                if b is not None and j % 4 == 0:
                    pe.wait_ge(xt_lo, 8 * b + 4 * t + j // 4 + 1)
                if last_order and j % 2 == 0:
                    pe.wait_ge(ot_lo, 8 * (0 if u < U_FOX else 1) + j // 2 + 1)

            def accumulator(u, i, t, j):
                ffn = ffn_part(u)
                if ffn is None:
                    m = mixer_unit(u)
                    if j == 0:
                        if u == U_FOX:
                            pe.wait_ge(y_added, 8 * (FG - 1) + 4 + t + 1)
                            pe.wait_ge(y_squared, 4 + t + 1)
                        elif m > 0:
                            pe.wait_ge(proj_read, 2 * (m - 1) + t + 1 + 6 * i)
                    return main[t]
                layer, g, part = ffn
                f = layer * FG + g
                if part < 2:
                    n = 2 * part + t
                    if j == 0:
                        if g > 0:
                            pe.wait_ge(y_added, 8 * (f - 1) + 4 + n + 1 + 8 * i)
                        elif part == 0:
                            pe.wait_ge(proj_read, 2 * mixer_unit(U_FFN[layer] - 1) + t + 1)
                    return main[n]
                n = j // 4
                if j % 4 == 0:
                    if t == 0:
                        pe.wait_ge(gate_read if n < 2 else hidden, 2 * f + n % 2 + 1 + 2 * i)
                    else:
                        pe.wait_ge(y_added, 8 * f + n + 1 + 8 * i)
                        if u in ENDS:
                            pe.wait_ge(y_squared, 8 * (ENDS[u] // 2 - 1) + n + 1)
                return main[n]

            def unit(u, i):
                ffn = ffn_part(u)
                G = attended(u)
                last_order = u in (U_SWA_OUT, U_FOX_OUT)
                when = LAST if last_order else STD
                down = ffn is not None and ffn[2] == 2
                for s in range(STEPS):
                    t, j = step_order(s, last_order)
                    n = u * UT + j
                    if t == 0:
                        pe.wait_ge(lo_ready, n + 1 + LT * i)
                    input_block(u, s, t, j, last_order)
                    if down and j == 0:
                        pe.wait_ge(ht_lo, 2 * (ffn[0] * FG + ffn[1]) + t + 1 + 2 * i)
                    dst = accumulator(u, i, t, j)
                    a_h, a_l, k = (h_hi, h_lo, j % 4) if down else (a_hi, a_lo, j)
                    n_k = 4 if down else KT
                    last = product(dst[:, :], a_h[:, k, tok(t)], a_l[:, k, tok(t)], ring_hi[:, n % RING, :], ring_lo[:, n % RING, :],
                                   k == 0, k == n_k - 1)
                    if t == 1:
                        last.then_inc(tile_used, 1)
                    elif k == n_k - 1:
                        if ffn is None:
                            done = proj_done
                        else:
                            done = (gate_done, up_done, down_done)[ffn[2]]
                        last.then_inc(done, 1)
                    if G is not None:
                        jj, odd = divmod(s - when["first"] - when["pt"], 2)
                        if odd == 0 and 0 <= jj < GH:
                            transpose_p(G, i, jj)
                        jj, odd = divmod(s - when["first"] - when["pv"], 2)
                        if odd == 0 and 0 <= jj < GH:
                            times_v(G, i, jj)
                        jj, odd = divmod(s - when["first"], 2)
                        if odd == 0 and 0 <= jj < GH:
                            scores(G, i, jj)
                        if s == when["o0"]:
                            transpose_o(G, i, 0)
                        if s == when["o1"]:
                            transpose_o(G, i, 1)
                    if ffn is None:
                        if holds_qk(u) and s == 24:
                            transpose_qk(u, i, 0)
                        if u > 0 and holds_qk(u - 1) and s == (when["tr"] if G is not None else STD["tr"]):
                            transpose_qk(u - 1, i, 1)
                        if u == U_FOX and s == 22:
                            forget_gate()
                        if u == U_FOX + 1 and s == 2:
                            cumulate()
                    else:
                        f = ffn[0] * FG + ffn[1]
                        if ffn[2] == 1 and s == 20:
                            hidden_transposes(f, i, 0)
                        if ffn[2] == 2 and s == 4:
                            hidden_transposes(f, i, 1)
                    if u in ENDS and ENDS[u] < 4 and s in (22, 25, 28, 31):
                        transpose_x(ENDS[u], 0, (s - 22) // 3)
                    if u - 1 in ENDS and s in (8, 10, 12, 14):
                        transpose_x(ENDS[u - 1], 1, (s - 8) // 2)

            pe.wait_ge(gains_loaded, 16)
            pe.wait_ge(consts_made, 2)
            nc.tensor.transpose(tr_ps[:, 0:P], gains_in[:, :], ident[:, :]).then_inc(gains_tr, 1)
            for t in range(NT):
                for q in range(NC_D):
                    transpose_x(0, t, q)
            whole_program(lambda n: pe.Fori(0, n), unit)


INPUTS = ["x", "positions", "norm_gains", "swa_w_in", "swa_sinks", "swa_w_out", "fox_w_in", "fox_b_f", "fox_w_out",
          "ffn_w_gate_up", "ffn_w_down"]


def kernel(**inputs):
    import concourse.bacc as bacc
    from concourse.bass_utils import run_bass_kernel_spmd

    nc = bacc.Bacc("TRN2", target_bir_lowering=False, num_devices=1)
    arrays = {name: np.ascontiguousarray(inputs[name]) for name in INPUTS}
    handles = [nc.dram_tensor(name, a.shape, mybir.dt.from_np(a.dtype), kind="ExternalInput").ap() for name, a in arrays.items()]
    result = nc.dram_tensor("out", arrays["x"].shape, F32, kind="ExternalOutput").ap()
    build(nc, *handles, result)
    return run_bass_kernel_spmd(nc, [arrays], core_ids=[0]).results[0]["out"]
```
